# Optimizing a Trainium2 kernel written in Bass

```python
import jax, jax.numpy as jnp
from jax import lax
import numpy as np

D_MODEL = 1024
BATCH = 1
SEQ = 1024
DEPTH = 1

HEAD_DIM = 64
N_HEADS_SB = 8
N_HEADS_SA = 8
N_KV_SA = 2
N_IDX_HEADS = 8
IDX_DIM = 64
TOPK_MAX = 256
ROPE_THETA = 500000.0
ROT_DIM = HEAD_DIM // 4
Q_BLOCK = 128
W_SB = N_HEADS_SB * HEAD_DIM
W_SA = N_HEADS_SA * HEAD_DIM
W_KV = N_KV_SA * HEAD_DIM
SPLIT_SIZES = (W_SB, W_SB, W_SB,
               W_SA, W_KV, W_KV,
               N_IDX_HEADS * IDX_DIM, IDX_DIM,
               N_IDX_HEADS,
               D_MODEL, D_MODEL)
IN_WIDTH = W_SB * 3 + W_SA + 2 * W_KV + N_IDX_HEADS * IDX_DIM + IDX_DIM + N_IDX_HEADS + 2 * D_MODEL

PEER_HEADS = 8
PEER_NKEYS = 128
PEER_EXPERTS = PEER_NKEYS * PEER_NKEYS
PEER_QDIM = 256
PEER_TOPK = 16
PEER_CHUNK = 128

NORM_EPS = 1e-6

kernel_name = "hybrid_stickbreak_dsa_peer_block"

def rmsnorm(x, g):
    xf = x.astype(jnp.float32)
    y = xf * lax.rsqrt(jnp.mean(xf * xf, axis=-1, keepdims=True) + NORM_EPS)
    return (y * g.astype(jnp.float32)).astype(x.dtype)

def partial_rope(x, positions):
    half = ROT_DIM // 2
    inv_freq = jnp.power(ROPE_THETA, -2.0 * jnp.arange(half, dtype=jnp.float32) / ROT_DIM)
    ang = positions.astype(jnp.float32)[..., None] * inv_freq
    cos = jnp.cos(ang)[:, :, None, :]
    sin = jnp.sin(ang)[:, :, None, :]
    xf = x.astype(jnp.float32)
    x1 = xf[..., :half]
    x2 = xf[..., half:ROT_DIM]
    out = jnp.concatenate([x1 * cos - x2 * sin, x2 * cos + x1 * sin, xf[..., ROT_DIM:]], axis=-1)
    return out.astype(x.dtype)

def stick_breaking_attention(q, k, v):
    B, T, H, d = q.shape
    scale = d ** -0.5
    kpos = jnp.arange(T)

    def block(i):
        t0 = i * Q_BLOCK
        qb = lax.dynamic_slice_in_dim(q, t0, Q_BLOCK, axis=1)
        z = jnp.einsum('bqhd,bshd->bhqs', qb, k).astype(jnp.float32) * scale
        qpos = t0 + jnp.arange(Q_BLOCK)
        strict = (kpos[None, :] < qpos[:, None])[None, None]
        log_fail = jnp.where(strict, jax.nn.log_sigmoid(-z), 0.0)
        between = lax.cumsum(log_fail, axis=3, reverse=True) - log_fail
        a = jnp.where(strict, jnp.exp(jax.nn.log_sigmoid(z) + between), 0.0)
        return jnp.einsum('bhqs,bshd->bqhd', a.astype(v.dtype), v)

    out = lax.map(block, jnp.arange(T // Q_BLOCK))
    return out.transpose(1, 0, 2, 3, 4).reshape(B, T, H, d)

def dsa_attention(q, k, v, q_idx, k_idx, w_idx):
    B, T, H, d = q.shape
    hkv = k.shape[2]
    groups = H // hkv
    k_sel = min(TOPK_MAX, T // 4)
    scale = d ** -0.5
    kpos = jnp.arange(T)
    gather = jax.vmap(lambda table, ids: table[ids])

    def block(i):
        t0 = i * Q_BLOCK
        qpos = t0 + jnp.arange(Q_BLOCK)
        qi = lax.dynamic_slice_in_dim(q_idx, t0, Q_BLOCK, axis=1)
        wi = lax.dynamic_slice_in_dim(w_idx, t0, Q_BLOCK, axis=1).astype(jnp.float32)
        rel = jax.nn.relu(jnp.einsum('bqhd,bsd->bqhs', qi, k_idx).astype(jnp.float32) * IDX_DIM ** -0.5)
        score = jnp.einsum('bqhs,bqh->bqs', rel, wi) * N_IDX_HEADS ** -0.5
        causal = (kpos[None, :] <= qpos[:, None])[None]
        score = jnp.where(causal, score, -jnp.inf)
        _, idx = lax.top_k(score, k_sel)
        valid = idx <= qpos[None, :, None]
        kg = gather(k, idx)
        vg = gather(v, idx)
        qb = lax.dynamic_slice_in_dim(q, t0, Q_BLOCK, axis=1).reshape(B, Q_BLOCK, hkv, groups, d)
        logits = jnp.einsum('bqhgd,bqkhd->bqhgk', qb, kg).astype(jnp.float32) * scale
        logits = jnp.where(valid[:, :, None, None, :], logits, -jnp.inf)
        p = jax.nn.softmax(logits, axis=-1)
        o = jnp.einsum('bqhgk,bqkhd->bqhgd', p.astype(v.dtype), vg)
        return o.reshape(B, Q_BLOCK, H * d)

    out = lax.map(block, jnp.arange(T // Q_BLOCK))
    return out.transpose(1, 0, 2, 3).reshape(B, T, H * d)

def token_mixer(h, positions, w_in, w_up_sb, w_up_sa, w_out):
    B, T, _ = h.shape
    proj = h @ w_in
    cuts = [int(s) for s in np.cumsum(SPLIT_SIZES)[:-1]]
    (q_sb, k_sb, v_sb, q_sa, k_sa, v_sa, q_ix, k_ix, w_ix, gate_sb, gate_sa) = jnp.split(proj, cuts, axis=-1)
    heads = lambda t, n: t.reshape(B, T, n, HEAD_DIM)
    o_sb = stick_breaking_attention(heads(q_sb, N_HEADS_SB), heads(k_sb, N_HEADS_SB), heads(v_sb, N_HEADS_SB))
    q_sa = partial_rope(heads(q_sa, N_HEADS_SA), positions)
    k_sa = partial_rope(heads(k_sa, N_KV_SA), positions)
    q_ix = partial_rope(q_ix.reshape(B, T, N_IDX_HEADS, IDX_DIM), positions)
    k_ix = partial_rope(k_ix[:, :, None, :], positions)[:, :, 0, :]
    o_sa = dsa_attention(q_sa, k_sa, heads(v_sa, N_KV_SA), q_ix, k_ix, w_ix)
    y_sb = o_sb.reshape(B, T, W_SB) @ w_up_sb
    y_sa = o_sa @ w_up_sa
    merged = jax.nn.sigmoid(gate_sb) * y_sb + jax.nn.sigmoid(gate_sa) * y_sa
    return merged @ w_out

def peer_ffn(h, w_query, sub_keys, expert_in, expert_out):
    B, T, D = h.shape
    n_tok = B * T
    xt = h.reshape(n_tok, D)
    q = (xt @ w_query).reshape(n_tok, PEER_HEADS, 2, PEER_QDIM // 2)
    s = jnp.einsum('nhpd,hpkd->nhpk', q, sub_keys).astype(jnp.float32)
    sv, si = lax.top_k(s, PEER_TOPK)
    cand = (sv[:, :, 0, :, None] + sv[:, :, 1, None, :]).reshape(n_tok, PEER_HEADS, PEER_TOPK * PEER_TOPK)
    cid = (si[:, :, 0, :, None] * PEER_NKEYS + si[:, :, 1, None, :]).reshape(n_tok, PEER_HEADS, PEER_TOPK * PEER_TOPK)
    top_s, top_p = lax.top_k(cand, PEER_TOPK)
    eid = jnp.take_along_axis(cid, top_p, axis=-1)
    g = jax.nn.softmax(top_s, axis=-1)
    n_chunks = n_tok // PEER_CHUNK

    def chunk(args):
        xc, ec, gc = args
        a = jnp.einsum('cd,chkd->chk', xc, expert_in[ec])
        act = gc.astype(xc.dtype) * jax.nn.gelu(a, approximate=False)
        return jnp.einsum('chk,chkd->cd', act, expert_out[ec])

    out = lax.map(chunk, (xt.reshape(n_chunks, PEER_CHUNK, D),
                          eid.reshape(n_chunks, PEER_CHUNK, PEER_HEADS, PEER_TOPK),
                          g.reshape(n_chunks, PEER_CHUNK, PEER_HEADS, PEER_TOPK)))
    return out.reshape(B, T, D)

def setup_inputs(seed: int = 0) -> dict:
    key = jax.random.key(seed)
    ks = jax.random.split(key, 20)
    f32 = jnp.float32
    nrm = lambda k, shape, s: jax.random.normal(k, shape, f32) * s
    D = D_MODEL
    x = jax.random.normal(ks[0], (BATCH, SEQ, D), f32)
    c = jax.random.normal(ks[1], (BATCH, D), f32)
    offsets = jax.random.randint(ks[2], (BATCH, 1), 0, 1024, dtype=jnp.int32)
    positions = jnp.arange(SEQ, dtype=jnp.int32)[None, :] + offsets
    return {
        "x": x,
        "c": c,
        "positions": positions,
        "w_ada": nrm(ks[3], (DEPTH, D, 6 * D), 0.5 * D ** -0.5),
        "b_ada": nrm(ks[4], (DEPTH, 6 * D), 0.02),
        "g_pre_mix": 1.0 + nrm(ks[5], (DEPTH, D), 0.02),
        "g_post_mix": 1.0 + nrm(ks[6], (DEPTH, D), 0.02),
        "w_in": nrm(ks[7], (DEPTH, D, IN_WIDTH), D ** -0.5),
        "w_up_sb": nrm(ks[8], (DEPTH, W_SB, D), W_SB ** -0.5),
        "w_up_sa": nrm(ks[9], (DEPTH, W_SA, D), W_SA ** -0.5),
        "w_out": nrm(ks[10], (DEPTH, D, D), D ** -0.5),
        "g_pre_ffn": 1.0 + nrm(ks[11], (DEPTH, D), 0.02),
        "g_post_ffn": 1.0 + nrm(ks[12], (DEPTH, D), 0.02),
        "w_peer_query": nrm(ks[13], (DEPTH, D, PEER_HEADS * PEER_QDIM), D ** -0.5),
        "peer_sub_keys": nrm(ks[14], (DEPTH, PEER_HEADS, 2, PEER_NKEYS, PEER_QDIM // 2), (PEER_QDIM // 2) ** -0.5),
        "peer_expert_in": nrm(ks[15], (DEPTH, PEER_EXPERTS, D), D ** -0.5),
        "peer_expert_out": nrm(ks[16], (DEPTH, PEER_EXPERTS, D), D ** -0.5),
    }

def reference(x, c, positions, w_ada, b_ada, g_pre_mix, g_post_mix, w_in, w_up_sb, w_up_sa, w_out,
              g_pre_ffn, g_post_ffn, w_peer_query, peer_sub_keys, peer_expert_in, peer_expert_out):
    for l in range(DEPTH):
        ada = jax.nn.silu(c) @ w_ada[l] + b_ada[l]
        shift1, scale1, gate1, shift2, scale2, gate2 = jnp.split(ada[:, None, :], 6, axis=-1)
        h = rmsnorm(x, g_pre_mix[l]) * (1.0 + scale1) + shift1
        y = token_mixer(h, positions, w_in[l], w_up_sb[l], w_up_sa[l], w_out[l])
        x = x + gate1 * rmsnorm(y, g_post_mix[l])
        h = rmsnorm(x, g_pre_ffn[l]) * (1.0 + scale2) + shift2
        y = peer_ffn(h, w_peer_query[l], peer_sub_keys[l], peer_expert_in[l], peer_expert_out[l])
        x = x + gate2 * rmsnorm(y, g_post_ffn[l])
    return x


_drawn_inputs = setup_inputs


def setup_inputs(seed=0):
    import zlib

    import numpy as np

    out = dict(_drawn_inputs(seed))
    spreads = {}
    factors = {}
    for name, (base, spread) in spreads.items():
        noise = np.random.default_rng([zlib.crc32(name.encode()), seed]).standard_normal(out[name].shape)
        drawn = base * np.exp(spread * noise) if base else spread * noise
        out[name] = __import__('jax').numpy.asarray(drawn.astype(out[name].dtype))
    for name, factor in factors.items():
        out[name] = (out[name] * factor).astype(out[name].dtype)
    return out
```

```python
from contextlib import ExitStack

import numpy as np

import concourse.bass as bass
from concourse import mybir

F32 = mybir.dt.float32
F32R = mybir.dt.float32r
U32 = mybir.dt.uint32
I32 = mybir.dt.int32
ALU = mybir.AluOpType
ACT = mybir.ActivationFunctionType
AX = mybir.AxisListType

P = 128
D = 1024
T = 1024
KC = D // P
NT = T // P
HALF = 512
NH = T // HALF
HD = 64
W_HEADS = 512
NPAIR = W_HEADS // P
Q_SB, K_SB, V_SB = 0, 512, 1024
Q_SA, K_SA, V_SA = 1536, 2048, 2176
Q_IX, K_IX, W_IX = 2304, 2816, 2880
G_SB, G_SA = 2888, 3912
TOPK = 256
EPS = 1e-6
SCALE = HD ** -0.5
NEG = -1.0e30
TAKEN = -3.0e38
PH = 8
NK = 128
PK = 16
CONST_COLS = {"ident": 128, "rot": 128, "tri": 128, "ones": 128, "strict": 128, "notstrict": 128,
              "causal": 128, "iota": 128, "iota16": 16, "freq": 1}


def shape_constants():
    r = np.arange(P)
    a, b = r[:, None], r[None, :]
    out = {"ident": (a == b) * 1.0}
    rot = np.zeros((P, P))
    for base in (0, HD):
        for i in range(8):
            rot[base + i + 8, base + i] = -1.0
            rot[base + i, base + i + 8] = 1.0
    out["rot"] = rot
    out["tri"] = -1.0 * (a >= b)
    out["ones"] = -np.ones((P, P))
    out["strict"] = 1.0 * (a < b)
    out["notstrict"] = NEG * (a >= b)
    out["causal"] = NEG * (b > a)
    out["iota"] = np.broadcast_to(b, (P, P)) * 1.0
    out["iota16"] = np.broadcast_to(np.arange(16), (P, 16)) * 1.0
    f = np.power(np.float32(500000.0), (-2.0 * np.arange(8, dtype=np.float32) / 16).astype(np.float32)).astype(np.float32)
    col = np.zeros((P, 1), np.float32)
    for base in (0, HD):
        col[base:base + 8, 0] = f
        col[base + 8:base + 16, 0] = f
    out["freq"] = col
    return np.concatenate([out[n].astype(np.float32) for n in CONST_COLS], axis=1)


class Linked:

    def __init__(self, eng, sem, base=0, apart=False):
        self.eng, self.sem, self.base, self.n, self.apart = eng, sem, base, 0, apart

    def __call__(self, ins):
        self.n += 1
        ins.then_inc(self.sem, 1)
        self.eng.wait_ge(self.sem, self.base + self.n)
        if self.apart:
            self.eng.nop(nofuse=True)


class Kit:

    def __init__(self, nc):
        self.nc = nc
        self.stack = ExitStack()

    def sem(self, name):
        return self.stack.enter_context(self.nc.semaphore(name))


def sbuf(nc, ctx, name, shape, dt=F32):
    return ctx.enter_context(nc.sbuf_tensor(name, shape, dt))


def psum(nc, ctx, name, shape, dt=F32):
    return ctx.enter_context(nc.psum_tensor(name, shape, dt))


def w_cols(w, c0, n):
    return w[:, bass.ds(c0, n)].rearrange("(k p) f -> p k f", p=P)


def ada_stage(nc, kit, I, consts, cols, gate_rows):
    NCH = 12
    with ExitStack() as ctx:
        rows = sbuf(nc, ctx, "ada_rows", [88, P])
        vec = sbuf(nc, ctx, "ada_vec", [P, 88])
        silu_c = sbuf(nc, ctx, "ada_silu", [P, KC])
        w = [sbuf(nc, ctx, f"ada_w{u}", [P, KC, HALF]) for u in range(4)]
        raw = sbuf(nc, ctx, "ada_raw", [P, 48])
        one = sbuf(nc, ctx, "ada_one", [P, 16])
        gate = sbuf(nc, ctx, "ada_gate", [P, 16])
        gout = sbuf(nc, ctx, "ada_gout", [16, P])
        ps_t = psum(nc, ctx, "ada_pt", [P, HALF])
        ps_a = psum(nc, ctx, "ada_pa", [P, HALF])
        vec_in, const_in, out_done = kit.sem("ada_vec_in"), kit.sem("ada_const_in"), kit.sem("ada_out")
        w_in = [kit.sem(f"ada_w_in{u}") for u in range(4)]
        turned, vec_ready, silu_ready, chunk_done, dve_order, gates_ready, gate_turned, gout_ready = (
            kit.sem("ada_" + n) for n in ("turned", "vec_ready", "silu", "chunk", "dve", "gates", "gturned", "gout"))
        ident = consts["ident"]
        block = ctx.enter_context(nc.Block())

        @block.sync
        def _(sp):
            sp.dma_start(consts["all"][:], I["consts"]).then_inc(const_in, 16)
            sp.dma_start(rows[0:8, :], I["c"].rearrange("b (k p) -> (b k) p", p=P)).then_inc(vec_in, 16)
            sp.dma_start(rows[8:56, :], I["b_ada"].rearrange("b (k p) -> (b k) p", p=P)).then_inc(vec_in, 16)
            for n, g in enumerate(("g_pre_mix", "g_post_mix", "g_pre_ffn", "g_post_ffn")):
                sp.dma_start(rows[56 + 8 * n:64 + 8 * n, :], I[g].rearrange("b (k p) -> (b k) p", p=P)).then_inc(vec_in, 16)
            with sp.Fori(0, NCH // 4) as i:
                for u in range(4):
                    sp.wait_ge(chunk_done, 4 * i)
                    sp.dma_start(w[u][:], w_cols(I["w_ada"][0], (i * 4 + u) * HALF, HALF)).then_inc(w_in[u], 16)

        @block.tensor
        def _(pe):
            pe.wait_ge(const_in, 16)
            pe.wait_ge(vec_in, 16 * 6)
            pe.transpose(ps_t[:, 0:88], rows[:, :], ident[0:88, 0:88]).then_inc(turned, 1)
            pe.wait_ge(silu_ready, 1)
            with pe.Fori(0, NCH // 4) as i:
                for u in range(4):
                    pe.wait_ge(w_in[u], 16 * i + 16)
                    for f in range(4):
                        for k in range(KC):
                            last = pe.matmul(ps_a[:, bass.ds((i * 4 + u) * 4 + f, 1)], w[u][:, k, f * P:(f + 1) * P],
                                             silu_c[:, k:k + 1], start=(k == 0), stop=(k == KC - 1))
                    last.then_inc(chunk_done, 1)
            pe.wait_ge(gates_ready, 1)
            pe.transpose(ps_t[0:16, 128:256], gate[:, :], ident[:, :]).then_inc(gate_turned, 1)

        @block.scalar
        def _(act):
            act.wait_ge(vec_ready, 1)
            act.activation(silu_c[:], vec[:, 0:8], ACT.Silu).then_inc(silu_ready, 1)
            act.wait_ge(gout_ready, 1)
            act.dma_start(gate_rows, gout[:]).then_inc(out_done, 16)
            act.wait_ge(out_done, 16)

        @block.vector
        def _(dve):
            link = Linked(dve, dve_order)
            dve.wait_ge(turned, 1)
            dve.tensor_copy(vec[:], ps_t[:, 0:88]).then_inc(vec_ready, 1)
            dve.wait_ge(vec_ready, 1)
            dve.wait_ge(chunk_done, NCH)
            link(dve.tensor_tensor(raw[:], ps_a[:, 0:48], vec[:, 8:56], ALU.add))
            link(dve.tensor_scalar(one[:, 0:8], raw[:, 8:16], 1.0, None, ALU.add))
            link(dve.tensor_scalar(one[:, 8:16], raw[:, 32:40], 1.0, None, ALU.add))
            link(dve.tensor_tensor(cols[:, 0:8], one[:, 0:8], vec[:, 56:64], ALU.mult))
            link(dve.tensor_copy(cols[:, 8:16], raw[:, 0:8]))
            link(dve.tensor_tensor(cols[:, 16:24], one[:, 8:16], vec[:, 72:80], ALU.mult))
            link(dve.tensor_copy(cols[:, 24:32], raw[:, 24:32]))
            link(dve.tensor_tensor(gate[:, 0:8], raw[:, 16:24], vec[:, 64:72], ALU.mult))
            dve.tensor_tensor(gate[:, 8:16], raw[:, 40:48], vec[:, 80:88], ALU.mult).then_inc(gates_ready, 1)
            dve.wait_ge(gate_turned, 1)
            dve.tensor_copy(gout[:], ps_t[0:16, 128:256]).then_inc(gout_ready, 1)


def pre_norm_stage(nc, kit, tag, x_rows, consts, mul_cols, add_cols, hT, lo=None):
    with ExitStack() as ctx:
        x = [sbuf(nc, ctx, f"{tag}_x{u}", [P, D]) for u in range(2)]
        sq = sbuf(nc, ctx, f"{tag}_sq", [P, D])
        ms = [sbuf(nc, ctx, f"{tag}_ms{u}", [P, 3]) for u in range(2)]
        ps = [psum(nc, ctx, f"{tag}_ps{u}", [P, KC, P]) for u in range(2)]
        x_in = [kit.sem(f"{tag}_x_in{u}") for u in range(2)]
        squares, roots, scaled, turned, evacuated, dve_order, act_order, eps_set = (
            kit.sem(f"{tag}_{n}") for n in ("squares", "roots", "scaled", "turned", "evac", "dve", "act", "eps"))
        eps = sbuf(nc, ctx, f"{tag}_epst", [P, 1])
        block = ctx.enter_context(nc.Block())

        @block.sync
        def _(sp):
            with sp.Fori(0, NT // 2) as i:
                for u in range(2):
                    sp.wait_ge(turned, 2 * i)
                    sp.dma_start(x[u][:], x_rows[bass.ds((i * 2 + u) * P, P), :]).then_inc(x_in[u], 16)

        @block.scalar
        def _(act):
            act.wait_ge(eps_set, 1)
            with act.Fori(0, NT // 2) as i:
                for u in range(2):
                    act.wait_ge(x_in[u], 16 * i + 16)
                    act.wait_ge(act_order, 2 * i + u)
                    act.wait_ge(scaled, 2 * i)
                    act.activation(sq[:], x[u][:], ACT.Square, accum_out=ms[u][:, 0:1]).then_inc(squares, 1)
                    act.wait_ge(squares, 2 * i + u + 1)
                    act.activation(ms[u][:, 1:2], ms[u][:, 0:1], ACT.Sqrt, bias=eps[:, 0:1], scale=1.0 / D).then_inc(act_order, 1)

        @block.vector
        def _(dve):
            dve.memset(eps[:], EPS).then_inc(eps_set, 1)
            with dve.Fori(0, NT // 2) as i:
                for u in range(2):
                    dve.wait_ge(act_order, 2 * i + u + 1)
                    dve.reciprocal(ms[u][:, 2:3], ms[u][:, 1:2]).then_inc(roots, 1)
                    dve.wait_ge(roots, 2 * i + u + 1)
                    dve.tensor_scalar(x[u][:], x[u][:], ms[u][:, 2:3], None, ALU.mult).then_inc(scaled, 1)
                    dve.wait_ge(turned, 2 * i + u + 1)
                    for k in range(KC):
                        last = dve.tensor_scalar(hT[:, k, bass.ds((i * 2 + u) * P, P)], ps[u][:, k, :],
                                                 mul_cols[:, k:k + 1], add_cols[:, k:k + 1], ALU.mult, ALU.add)
                    last.then_inc(evacuated, 1)

        @block.tensor
        def _(pe):
            with pe.Fori(0, NT // 2) as i:
                for u in range(2):
                    pe.wait_ge(scaled, 2 * i + u + 1)
                    pe.wait_ge(evacuated, 2 * i)
                    for k in range(KC):
                        last = pe.transpose(ps[u][:, k, :], x[u][:, k * P:(k + 1) * P], consts["ident"][:, :])
                    last.then_inc(turned, 1)


def project_T(pe, out, w, hT):
    for half in range(NH):
        for k in range(KC):
            last = pe.matmul(out[:, half, :], w[:, k, :], hT[:, k, half * HALF:(half + 1) * HALF],
                             start=(k == 0), stop=(k == KC - 1))
    return last


def rotate(pe, out, rot, src):
    for half in range(NH):
        last = pe.matmul(out[:, half, :], rot[:, :], src[:, half * HALF:(half + 1) * HALF], start=True, stop=True)
    return last


def flat(bank2):
    return bank2[:].rearrange("p h c -> p (h c)")


def indexer_stage(nc, kit, I, consts, hT, cosT, sinT, scores):
    TWO_PI = 2 * np.pi
    C1 = 6.28125
    C2 = float(np.float32(np.round((TWO_PI - C1) * 2 ** 20) / 2 ** 20))
    C3 = float(np.float32(TWO_PI - C1 - C2))
    MAGIC = 1.5 * 2 ** 23
    PI_LOW = 3.1415925
    STEPS = 2 * NT
    with ExitStack() as ctx:
        pos_i = sbuf(nc, ctx, "ix_pos_i", [P, T], I32)
        ang = sbuf(nc, ctx, "ix_ang", [P, T])
        turn = sbuf(nc, ctx, "ix_turn", [P, T])
        wk = sbuf(nc, ctx, "ix_wk", [P, KC, P])
        ww = sbuf(nc, ctx, "ix_ww", [P, KC, 8])
        wq = sbuf(nc, ctx, "ix_wq", [P, KC, P])
        kT = sbuf(nc, ctx, "ix_kT", [P, T])
        qT = sbuf(nc, ctx, "ix_qT", [P, T])
        raw = sbuf(nc, ctx, "ix_raw", [P, T])
        tmp = sbuf(nc, ctx, "ix_tmp", [P, T])
        head_w = sbuf(nc, ctx, "ix_head_w", [P, NT * 8])
        rel = [sbuf(nc, ctx, f"ix_rel{u}", [P, T]) for u in range(2)]
        ps_p = psum(nc, ctx, "ix_pp", [P, 2, HALF])
        ps_r = psum(nc, ctx, "ix_pr", [P, 2, HALF])
        ps_s = [psum(nc, ctx, f"ix_ps{u}", [P, 2, HALF]) for u in range(2)]
        (pos_in, wk_in, ww_in, wq_in, proj_done, raw_ready, rot_done, rope_done, hw_done, hw_ready, sc_done,
         rel_done, acc_done, dve_order, angle_ready, table_ready) = (
            kit.sem("ix_" + n) for n in ("pos_in", "wk_in", "ww_in", "wq_in", "proj", "raws", "rotd", "rope", "hwd",
                                         "hwr", "sc", "reld", "acc", "dve", "angle", "table"))
        block = ctx.enter_context(nc.Block())

        @block.sync
        def _(sp):
            sp.dma_start(pos_i[:], I["positions"].partition_broadcast(P)).then_inc(pos_in, 16)
            for e in range(2):
                sp.dma_start(wk[:, :, e * HD:(e + 1) * HD], w_cols(I["w_in"][0], K_IX, HD)).then_inc(wk_in, 16)
            sp.dma_start(ww[:], w_cols(I["w_in"][0], W_IX, 8)).then_inc(ww_in, 16)
            with sp.Fori(0, NPAIR) as p:
                sp.wait_ge(proj_done, p + 1)
                sp.dma_start(wq[:], w_cols(I["w_in"][0], p * P + Q_IX, P)).then_inc(wq_in, 16)

        @block.tensor
        def _(pe):
            pe.wait_ge(wk_in, 32)
            project_T(pe, ps_p, wk, hT).then_inc(proj_done, 1)
            pe.wait_ge(ww_in, 16)
            for t in range(NT):
                for k in range(KC):
                    last = pe.matmul(ps_s[0][:, 0, t * 8:(t + 1) * 8], hT[:, k, t * P:(t + 1) * P], ww[:, k, :],
                                     start=(k == 0), stop=(k == KC - 1))
            last.then_inc(hw_done, 1)
            pe.wait_ge(raw_ready, 1)
            rotate(pe, ps_r, consts["rot"], raw).then_inc(rot_done, 1)
            pe.wait_ge(hw_ready, 1)
            with pe.Fori(0, NPAIR) as p:
                pe.wait_ge(wq_in, 16 * p + 16)
                project_T(pe, ps_p, wq, hT).then_inc(proj_done, 1)
                pe.wait_ge(raw_ready, p + 2)
                pe.wait_ge(rope_done, p + 1)
                rotate(pe, ps_r, consts["rot"], raw).then_inc(rot_done, 1)
                pe.wait_ge(rope_done, p + 2)
                for n in range(STEPS):
                    t, e = n // 2, n % 2
                    pe.wait_ge(rel_done, STEPS * p + max(n - 1, 0))
                    L = (t + 1) * P
                    for c0 in range(0, L, HALF):
                        last = pe.matmul(ps_s[n % 2][:, c0 // HALF, 0:min(HALF, L - c0)],
                                         qT[e * HD:(e + 1) * HD, t * P:(t + 1) * P],
                                         kT[e * HD:(e + 1) * HD, c0:min(c0 + HALF, L)], start=True, stop=True)
                    last.then_inc(sc_done, 1)

        @block.scalar
        def _(act):
            act.wait_ge(angle_ready, 1)
            act.activation(sinT[:], turn[:], ACT.Sin).then_inc(table_ready, 1)
            act.wait_ge(angle_ready, 2)
            act.activation(cosT[:], tmp[:], ACT.Sin).then_inc(table_ready, 1)
            act.wait_ge(proj_done, 1)
            act.copy(raw[:], flat(ps_p)).then_inc(raw_ready, 1)
            with act.Fori(0, NPAIR) as p:
                act.wait_ge(proj_done, p + 2)
                act.wait_ge(rope_done, p + 1)
                act.copy(raw[:], flat(ps_p)).then_inc(raw_ready, 1)
                for n in range(STEPS):
                    L = (n // 2 + 1) * P
                    act.wait_ge(sc_done, STEPS * p + n + 1)
                    act.wait_ge(acc_done, STEPS * p + max(n - 1, 0))
                    act.activation(rel[n % 2][:, 0:L], flat(ps_s[n % 2])[:, 0:L], ACT.Relu, scale=SCALE).then_inc(rel_done, 1)

        @block.vector
        def _(dve):
            link = Linked(dve, dve_order)
            dve.wait_ge(pos_in, 16)
            link(dve.tensor_copy(ang[:], pos_i[:]))
            link(dve.tensor_scalar(ang[:], ang[:], consts["freq"][:, 0:1], None, ALU.mult))
            for shift, dst in ((0.0, turn), (0.25, tmp)):
                link(dve.tensor_scalar(rel[0][:], ang[:], 1.0 / TWO_PI, shift, ALU.mult, ALU.add))
                link(dve.tensor_scalar(rel[0][:], rel[0][:], MAGIC, None, ALU.add))
                link(dve.tensor_scalar(rel[0][:], rel[0][:], -MAGIC, None, ALU.add))
                link(dve.scalar_tensor_tensor(rel[1][:], rel[0][:], -C1, ang[:], ALU.mult, ALU.add))
                link(dve.scalar_tensor_tensor(rel[1][:], rel[0][:], -C2, rel[1][:], ALU.mult, ALU.add))
                link(dve.scalar_tensor_tensor(rel[1][:], rel[0][:], -C3, rel[1][:], ALU.mult, ALU.add))
                link(dve.tensor_scalar(rel[1][:], rel[1][:], shift * TWO_PI, PI_LOW, ALU.add, ALU.min))
                dve.tensor_scalar(dst[:], rel[1][:], -PI_LOW, None, ALU.max).then_inc(angle_ready, 1)
            dve.wait_ge(table_ready, 2)
            dve.wait_ge(hw_done, 1)
            dve.tensor_scalar(head_w[:], ps_s[0][:, 0, 0:NT * 8], 8 ** -0.5, None, ALU.mult).then_inc(hw_ready, 1)
            link(dve.memset(scores[:], 0.0))
            dve.wait_ge(rot_done, 1)
            dve.wait_ge(angle_ready, 2)
            link(dve.tensor_tensor(kT[:], raw[:], cosT[:], ALU.mult))
            link(dve.tensor_tensor(tmp[:], flat(ps_r), sinT[:], ALU.mult))
            dve.tensor_tensor(kT[:], kT[:], tmp[:], ALU.add).then_inc(rope_done, 1)
            dve.wait_ge(hw_ready, 1)
            done = link.n
            with dve.Fori(0, NPAIR) as p:
                link = Linked(dve, dve_order, done + p * 2)
                dve.wait_ge(rot_done, p + 2)
                dve.wait_ge(sc_done, STEPS * p)
                dve.wait_ge(rope_done, p + 1)
                link(dve.tensor_tensor(qT[:], raw[:], cosT[:], ALU.mult))
                link(dve.tensor_tensor(tmp[:], flat(ps_r), sinT[:], ALU.mult))
                dve.tensor_tensor(qT[:], qT[:], tmp[:], ALU.add).then_inc(rope_done, 1)
                for n in range(STEPS):
                    t, e = n // 2, n % 2
                    L = (t + 1) * P
                    dve.wait_ge(rel_done, STEPS * p + n + 1)
                    dve.wait_ge(acc_done, STEPS * p + n)
                    dve.scalar_tensor_tensor(scores[:, t, 0:L], rel[n % 2][:, 0:L], head_w[:, bass.ds(p * 2 + (t * 8 + e), 1)],
                                             scores[:, t, 0:L], ALU.mult, ALU.add).then_inc(acc_done, 1)


def stick_stage(nc, kit, I, consts, hT, oT):
    steps = []
    for e in range(2):
        for c in range(NH):
            for s in range(4 * c + 3, -1, -1):
                steps.append((e, c, s, max(0, (s - 4 * c) * P), s == 4 * c + 3, s == 0))
    N = len(steps)
    with ExitStack() as ctx:
        wq = sbuf(nc, ctx, "sb_wq", [P, KC, P])
        wk = sbuf(nc, ctx, "sb_wk", [P, KC, P])
        wv = sbuf(nc, ctx, "sb_wv", [P, KC, P])
        qT = sbuf(nc, ctx, "sb_qT", [P, T])
        kT = sbuf(nc, ctx, "sb_kT", [P, T])
        v = sbuf(nc, ctx, "sb_v", [P, NT, P])
        soft = [sbuf(nc, ctx, f"sb_soft{u}", [P, HALF]) for u in range(2)]
        m = [sbuf(nc, ctx, f"sb_m{u}", [P, HALF]) for u in range(2)]
        later = [sbuf(nc, ctx, f"sb_later{u}", [P, HALF]) for u in range(2)]
        a = [sbuf(nc, ctx, f"sb_a{u}", [P, HALF]) for u in range(2)]
        zeros = sbuf(nc, ctx, "sb_zeros", [P, HALF])
        ps_p = psum(nc, ctx, "sb_pp", [P, 2, HALF])
        ps_z = [psum(nc, ctx, f"sb_pz{u}", [P, HALF]) for u in range(4)]
        ps_o = [psum(nc, ctx, f"sb_po{u}", [P, HALF]) for u in range(2)]
        (w_loaded, proj_done, proj_read, z_done, soft_done, m_done, e_done, a_done, o_done, o_read, act_order,
         dve_order, later_done) = (
            kit.sem("sb_" + n) for n in ("w", "proj", "projr", "z", "soft", "m", "e", "a", "o", "or", "act", "dve", "later"))
        pool_order = kit.sem("sb_pool")
        wv_loaded, wk_loaded = kit.sem("sb_wv_in"), kit.sem("sb_wk_in")
        block = ctx.enter_context(nc.Block())

        @block.sync
        def _(sp):
            with sp.Fori(0, NPAIR) as p:
                sp.wait_ge(proj_done, 3 * p)
                sp.dma_start(wq[:], w_cols(I["w_in"][0], p * P + Q_SB, P)).then_inc(w_loaded, 16)
                sp.dma_start(wk[:], w_cols(I["w_in"][0], p * P + K_SB, P)).then_inc(wk_loaded, 16)
                sp.dma_start(wv[:], w_cols(I["w_in"][0], p * P + V_SB, P)).then_inc(wv_loaded, 16)

        @block.tensor
        def _(pe):
            with pe.Fori(0, NPAIR) as p:
                pe.wait_ge(w_loaded, 16 * p + 16)
                pe.wait_ge(proj_read, 3 * p)
                project_T(pe, ps_p, wq, hT).then_inc(proj_done, 1)
                pe.wait_ge(wk_loaded, 16 * p + 16)
                pe.wait_ge(proj_read, 3 * p + 1)
                project_T(pe, ps_p, wk, hT).then_inc(proj_done, 1)
                pe.wait_ge(wv_loaded, 16 * p + 16)
                pe.wait_ge(proj_read, 3 * p + 2)
                for t in range(NT):
                    for k in range(KC):
                        last = pe.matmul(ps_p[:, t // 4, (t % 4) * P:(t % 4 + 1) * P], hT[:, k, t * P:(t + 1) * P],
                                         wv[:, k, :], start=(k == 0), stop=(k == KC - 1))
                last.then_inc(proj_done, 1)

                def scores(n):
                    e, c, s, lo, _, _ = steps[n]
                    pe.wait_ge(a_done, N * p + max(n - 3, 0))
                    pe.matmul(ps_z[n % 4][:, lo:HALF], kT[e * HD:(e + 1) * HD, s * P:(s + 1) * P],
                              qT[e * HD:(e + 1) * HD, c * HALF + lo:(c + 1) * HALF], start=True, stop=True,
                              skip_group_check=True).then_inc(z_done, 1)

                def sums(n):
                    e, c, s, lo, first, _ = steps[n]
                    pe.wait_ge(m_done, N * p + n + 1)
                    z = ps_z[n % 4]
                    last = pe.matmul(z[:, lo:HALF], consts["tri"][:, :], m[n % 2][:, lo:HALF], start=False, stop=True,
                                     skip_group_check=True)
                    if s >= 4 * c:
                        last = pe.matmul(z[:, lo:lo + P], consts["ident"][:, :], consts["notstrict"][:, :], start=False,
                                         stop=True, skip_group_check=True)
                    if not first:
                        pe.wait_ge(later_done, N * p + n)
                        last = pe.matmul(z[:, lo:HALF], consts["ones"][:, :], later[n % 2][:, lo:HALF], start=False,
                                         stop=True, skip_group_check=True)
                    last.then_inc(e_done, 1)

                def values(n):
                    e, c, s, lo, first, last_s = steps[n]
                    pe.wait_ge(a_done, N * p + n + 1)
                    g = 2 * e + c
                    if first:
                        pe.wait_ge(o_read, 4 * p + max(g - 1, 0))
                    ins = pe.matmul(ps_o[g % 2][:, lo:HALF], v[:, s, :], a[n % 2][:, lo:HALF], start=first, stop=last_s,
                                    skip_group_check=True)
                    ins.then_inc(o_done, 1)

                pe.wait_ge(proj_read, 3 * p + 3)
                scores(0)
                scores(1)
                for n in range(N):
                    if n + 2 < N:
                        scores(n + 2)
                    if n >= 1:
                        values(n - 1)
                    sums(n)
                values(N - 1)

        @block.scalar
        def _(act):
            with act.Fori(0, NPAIR) as p:
                act.wait_ge(proj_done, 3 * p + 1)
                act.wait_ge(z_done, N * p)
                act.activation(qT[:], flat(ps_p), ACT.Copy, scale=SCALE).then_inc(proj_read, 1)
                act.wait_ge(proj_done, 3 * p + 2)
                act.copy(kT[:], flat(ps_p)).then_inc(proj_read, 1)
                act.wait_ge(proj_done, 3 * p + 3)
                act.wait_ge(o_done, N * p)
                act.copy(v[:].rearrange("p t f -> p (t f)"), flat(ps_p)).then_inc(proj_read, 1)

                def soft_part(n):
                    lo = steps[n][3]
                    link = Linked(act, act_order, 2 * N * p + 2 * n)
                    act.wait_ge(z_done, N * p + n + 1)
                    act.wait_ge(m_done, N * p + max(n - 1, 0))
                    s = soft[n % 2][:, lo:HALF]
                    link(act.activation(s, ps_z[n % 4][:, lo:HALF], ACT.Abs))
                    link(act.activation(s, s, ACT.Exp, scale=-1.0))
                    act.activation(s, s, ACT.Ln, bias=1.0).then_inc(soft_done, 1)

                soft_part(0)
                for n in range(N):
                    if n + 1 < N:
                        soft_part(n + 1)
                    lo = steps[n][3]
                    act.wait_ge(e_done, N * p + n + 1)
                    act.wait_ge(o_done, N * p + max(n - 1, 0))
                    act.activation(a[n % 2][:, lo:HALF], ps_z[n % 4][:, lo:HALF], ACT.Exp).then_inc(a_done, 1)

        @block.vector
        def _(dve):
            with dve.Fori(0, NPAIR) as p:
                def evacuate(g):
                    e, c = g // 2, g % 2
                    end = max(n for n in range(N) if steps[n][0:2] == (e, c)) + 1
                    dve.wait_ge(o_done, N * p + end)
                    dve.tensor_copy(oT[e * HD:(e + 1) * HD, p, c * HALF:(c + 1) * HALF],
                                    ps_o[g % 2][e * HD:(e + 1) * HD, :]).then_inc(o_read, 1)

                for n in range(N):
                    e, c, s, lo, first, _ = steps[n]
                    dve.wait_ge(soft_done, N * p + n + 1)
                    dve.wait_ge(e_done, N * p + max(n - 1, 0))
                    dve.wait_ge(later_done, N * p + max(n - 1, 0))
                    diag = s >= 4 * c
                    ins = dve.scalar_tensor_tensor(m[n % 2][:, lo:HALF], ps_z[n % 4][:, lo:HALF], 0.0,
                                                   soft[n % 2][:, lo:HALF], ALU.max, ALU.add)
                    if diag:
                        ins.then_inc(dve_order, 1)
                        nd = sum(1 for q in steps[:n + 1] if q[2] >= 4 * q[1])
                        dve.wait_ge(dve_order, 16 * p + nd)
                        ins = dve.tensor_tensor(m[n % 2][:, lo:lo + P], m[n % 2][:, lo:lo + P], consts["strict"][:, :], ALU.mult)
                    ins.then_inc(m_done, 1)
                    g = 2 * e + c
                    if first and g >= 1:
                        evacuate(g - 1)
                evacuate(3)

        @block.gpsimd
        def _(pool):
            pool.memset(zeros[:], 0.0).then_inc(pool_order, 1)
            pool.wait_ge(pool_order, 1)
            with pool.Fori(0, NPAIR) as p:
                for n in range(N):
                    e, c, s, lo, first, last_s = steps[n]
                    pool.wait_ge(m_done, N * p + n + 1)
                    pool.wait_ge(e_done, N * p + n)
                    pool.wait_ge(later_done, N * p + n)
                    pool.nop(nofuse=True)
                    dst = later[(n + 1) % 2]
                    if lo:
                        count = sum(1 for q in steps[:n + 1] if q[3])
                        pool.tensor_copy(dst[:, 0:lo], zeros[:, 0:lo]).then_inc(pool_order, 1)
                        pool.wait_ge(pool_order, 12 * p + (count + 1))
                        pool.nop(nofuse=True)
                    if last_s:
                        ins = pool.tensor_copy(dst[:, 0:P], zeros[:, 0:P])
                    elif first:
                        ins = pool.tensor_copy(dst[:, lo:HALF], m[n % 2][:, lo:HALF])
                    else:
                        ins = pool.tensor_tensor(dst[:, lo:HALF], later[n % 2][:, lo:HALF], m[n % 2][:, lo:HALF], ALU.add)
                    ins.then_inc(later_done, 1)


def select_stage(nc, kit, consts, scores):
    with ExitStack() as ctx:
        top = sbuf(nc, ctx, "sel_top", [P, 8])
        dve_order = kit.sem("sel_dve")
        block = ctx.enter_context(nc.Block())

        @block.vector
        def _(dve):
            link = Linked(dve, dve_order)
            for t in range(NT):
                L = (t + 1) * P
                if t < TOPK // P:
                    link(dve.memset(scores[:, t, 0:L], 0.0))
                link(dve.tensor_tensor(scores[:, t, L - P:L], scores[:, t, L - P:L], consts["causal"][:, :], ALU.add))
            done = link.n
            for t in range(TOPK // P, NT):
                row = scores[:, t, 0:(t + 1) * P]
                with dve.Fori(0, TOPK // 8) as r:
                    link = Linked(dve, dve_order, done + r * 2, apart=True)
                    link(dve.max(top[:], row))
                    link(dve.match_replace(row, top[:], row, TAKEN))
                done += 2 * (TOPK // 8)
                link = Linked(dve, dve_order, done)
                link(dve.tensor_scalar(row, row, TAKEN, NEG, ALU.not_equal, ALU.mult))
                done += 1


def sparse_stage(nc, kit, I, consts, hT, cosT, sinT, mask, oT):
    NKV = 2
    steps = [(j, t, e) for j in range(2) for t in range(NT) for e in range(2)]
    N = len(steps)
    with ExitStack() as ctx:
        wk = sbuf(nc, ctx, "sa_wk", [P, KC, P])
        wv = sbuf(nc, ctx, "sa_wv", [P, KC, HD])
        wq = sbuf(nc, ctx, "sa_wq", [P, KC, P])
        kT = sbuf(nc, ctx, "sa_kT", [P, T])
        qT = sbuf(nc, ctx, "sa_qT", [P, T])
        v = sbuf(nc, ctx, "sa_v", [P, NT, HD])
        raw = sbuf(nc, ctx, "sa_raw", [P, T])
        tmp = sbuf(nc, ctx, "sa_tmp", [P, T])
        logit = [sbuf(nc, ctx, f"sa_logit{u}", [P, T]) for u in range(2)]
        prob = [sbuf(nc, ctx, f"sa_prob{u}", [P, T]) for u in range(2)]
        probT = [sbuf(nc, ctx, f"sa_probT{u}", [P, T]) for u in range(2)]
        stat = [sbuf(nc, ctx, f"sa_stat{u}", [P, 4]) for u in range(2)]
        o = [sbuf(nc, ctx, f"sa_o{u}", [P, P]) for u in range(2)]
        ps_l = [psum(nc, ctx, f"sa_pl{u}", [P, 2, HALF]) for u in range(2)]
        ps_t = psum(nc, ctx, "sa_pt", [P, 2, HALF])
        ps_o = psum(nc, ctx, "sa_po", [P, HALF])
        ps_x = psum(nc, ctx, "sa_px", [P, HALF])
        (wk_in, wv_in, wq_in, proj_done, raw_ready, rot_done, rope_done, l_done, l_read, max_done, p_done, t_done,
         t_read, o_done, o_read, x_done, x_read, dve_order, v_done, v_read, act_order) = (
            kit.sem("sa_" + n) for n in ("wk", "wv", "wq", "proj", "raws", "rots", "rope", "l", "lr", "max", "p", "t",
                                         "tr", "o", "or", "x", "xr", "dve", "v", "vr", "act"))
        block = ctx.enter_context(nc.Block())

        @block.sync
        def _(sp):
            with sp.Fori(0, NKV) as g:
                sp.wait_ge(proj_done, 3 * g)
                for e in range(2):
                    sp.dma_start(wk[:, :, e * HD:(e + 1) * HD], w_cols(I["w_in"][0], g * HD + K_SA, HD)).then_inc(wk_in, 16)
                sp.wait_ge(v_done, g)
                sp.dma_start(wv[:], w_cols(I["w_in"][0], g * HD + V_SA, HD)).then_inc(wv_in, 16)
                for j in range(2):
                    sp.wait_ge(proj_done, 3 * g + 2 * j)
                    sp.dma_start(wq[:], w_cols(I["w_in"][0], (g * 2 + j) * P + Q_SA, P)).then_inc(wq_in, 16)

        @block.tensor
        def _(pe):
            def rope(g, k):
                project_T(pe, ps_l[0], wk if k == 0 else wq, hT).then_inc(proj_done, 1)
                pe.wait_ge(raw_ready, 3 * g + k + 1)
                rotate(pe, ps_l[1], consts["rot"], raw).then_inc(rot_done, 1)
                pe.wait_ge(rope_done, 3 * g + k + 1)

            with pe.Fori(0, NKV) as g:
                pe.wait_ge(wk_in, 32 * g + 32)
                pe.wait_ge(l_read, N * g)
                rope(g, 0)
                pe.wait_ge(wv_in, 16 * g + 16)
                for t in range(NT):
                    for k in range(KC):
                        last = pe.matmul(ps_o[:, t * HD:(t + 1) * HD], hT[:, k, t * P:(t + 1) * P], wv[:, k, :],
                                         start=(k == 0), stop=(k == KC - 1))
                last.then_inc(v_done, 1)

                def logits(n):
                    j, t, e = steps[n]
                    pe.wait_ge(l_read, N * g + max(n - 1, 0))
                    L = (t + 1) * P
                    for c0 in range(0, L, HALF):
                        last = pe.matmul(ps_l[n % 2][:, c0 // HALF, 0:min(HALF, L - c0)],
                                         qT[e * HD:(e + 1) * HD, t * P:(t + 1) * P],
                                         kT[e * HD:(e + 1) * HD, c0:min(c0 + HALF, L)], start=True, stop=True)
                    last.then_inc(l_done, 1)

                def turn(n):
                    j, t, e = steps[n]
                    pe.wait_ge(p_done, N * g + n + 1)
                    pe.wait_ge(t_read, N * g + n)
                    for s in range(t + 1):
                        last = pe.transpose(ps_t[:, s // 4, (s % 4) * P:(s % 4 + 1) * P], prob[n % 2][:, s * P:(s + 1) * P],
                                            consts["ident"][:, :])
                    last.then_inc(t_done, 1)

                def values(n):
                    j, t, e = steps[n]
                    pe.wait_ge(t_read, N * g + n + 1)
                    pe.wait_ge(o_read, N * g + n)
                    pe.wait_ge(v_read, g + 1)
                    for s in range(t + 1):
                        last = pe.matmul(ps_o[:, 0:HD], probT[n % 2][:, s * P:(s + 1) * P], v[:, s, :], start=(s == 0), stop=(s == t))
                    last.then_inc(o_done, 1)

                def out_turn(n):
                    if n % 2:
                        pe.wait_ge(o_read, N * g + n + 1)
                        pe.wait_ge(x_read, (N // 2) * g + n // 2)
                        pe.transpose(ps_x[:, 0:P], o[(n // 2) % 2][:, :], consts["ident"][:, :]).then_inc(x_done, 1)

                for j in range(2):
                    pe.wait_ge(wq_in, 32 * g + 16 * j + 16)
                    pe.wait_ge(l_read, N * g + 16 * j)
                    rope(g, 1 + j)
                    lo, hi = 16 * j, 16 * j + 16
                    logits(lo)
                    for n in range(lo, hi + 2):
                        if n + 1 < hi:
                            logits(n + 1)
                        if n < hi:
                            turn(n)
                        if lo <= n - 1 < hi:
                            values(n - 1)
                        if lo <= n - 2:
                            out_turn(n - 2)

        @block.scalar
        def _(act):
            with act.Fori(0, NKV) as g:
                def copy_raw(k):
                    act.wait_ge(proj_done, 3 * g + k + 1)
                    act.wait_ge(rope_done, 3 * g + k)
                    act.copy(raw[:], flat(ps_l[0])).then_inc(raw_ready, 1)

                copy_raw(0)
                act.wait_ge(v_done, g + 1)
                act.copy(v[:].rearrange("p t f -> p (t f)"), ps_o[:, :]).then_inc(v_read, 1)
                for j in range(2):
                    copy_raw(1 + j)
                    lo, hi = 16 * j, 16 * j + 16

                    def turned_copy(n):
                        L = (steps[n][1] + 1) * P
                        act.wait_ge(t_done, N * g + n + 1)
                        act.wait_ge(o_done, N * g + max(n - 1, 0))
                        act.copy(probT[n % 2][:, 0:L], flat(ps_t)[:, 0:L]).then_inc(t_read, 1)

                    for n in range(lo, hi):
                        L = (steps[n][1] + 1) * P
                        act.wait_ge(max_done, N * g + n + 1)
                        act.wait_ge(t_done, N * g + max(n - 1, 0))
                        act.wait_ge(o_read, N * g + max(n - 1, 0))
                        act.activation(prob[n % 2][:, 0:L], logit[n % 2][:, 0:L], ACT.Exp, bias=stat[n % 2][:, 0:1],
                                       accum_out=stat[n % 2][:, 1:2]).then_inc(p_done, 1)
                        if n > lo:
                            turned_copy(n - 1)
                    turned_copy(hi - 1)

        @block.vector
        def _(dve):
            PER = 6 + 2 * N
            with dve.Fori(0, NKV) as g:
                link = Linked(dve, dve_order, g * PER)

                def rope(k, dst, scale):
                    dve.wait_ge(rot_done, 3 * g + k + 1)
                    link(dve.scalar_tensor_tensor(dst[:], raw[:], scale, cosT[:], ALU.mult, ALU.mult))
                    link(dve.scalar_tensor_tensor(tmp[:], flat(ps_l[1]), scale, sinT[:], ALU.mult, ALU.mult))
                    dve.tensor_tensor(dst[:], dst[:], tmp[:], ALU.add).then_inc(rope_done, 1)

                dve.wait_ge(l_done, N * g)
                rope(0, kT, 1.0)
                for j in range(2):
                    dve.wait_ge(l_done, N * g + 16 * j)
                    rope(1 + j, qT, SCALE)
                    lo, hi = 16 * j, 16 * j + 16

                    def output(n):
                        _, t, e = steps[n]
                        dve.wait_ge(p_done, N * g + n + 1)
                        link(dve.reciprocal(stat[n % 2][:, 2:3], stat[n % 2][:, 1:2]))
                        dve.wait_ge(o_done, N * g + n + 1)
                        dve.wait_ge(x_done, (N // 2) * g + max(n // 2 - 1, 0))
                        dve.tensor_scalar(o[(n // 2) % 2][:, e * HD:(e + 1) * HD], ps_o[:, 0:HD], stat[n % 2][:, 2:3], None,
                                          ALU.mult).then_inc(o_read, 1)

                    def keep(n):
                        if n % 2:
                            t = steps[n][1]
                            dve.wait_ge(x_done, (N // 2) * g + n // 2 + 1)
                            dve.tensor_copy(oT[:, g * 2 + j, t * P:(t + 1) * P], ps_x[:, 0:P]).then_inc(x_read, 1)

                    for n in range(lo, hi + 2):
                        if n < hi:
                            t = steps[n][1]
                            L = (t + 1) * P
                            dve.wait_ge(l_done, N * g + n + 1)
                            dve.wait_ge(p_done, N * g + max(n - 1, 0))
                            dve.tensor_tensor(logit[n % 2][:, 0:L], flat(ps_l[n % 2])[:, 0:L], mask[:, t, 0:L], ALU.add).then_inc(l_read, 1)
                            dve.wait_ge(l_read, N * g + n + 1)
                            link(dve.tensor_reduce(stat[n % 2][:, 3:4], logit[n % 2][:, 0:L], AX.X, ALU.max))
                            dve.tensor_scalar(stat[n % 2][:, 0:1], stat[n % 2][:, 3:4], -1.0, None, ALU.mult).then_inc(max_done, 1)
                        if lo <= n - 1 < hi:
                            output(n - 1)
                        if lo <= n - 2:
                            keep(n - 2)
                assert link.n == PER, link.n


def merge_stage(nc, kit, I, hT, oT_sb, oT_sa, gate_rows, x1):
    with ExitStack() as ctx:
        wout = sbuf(nc, ctx, "mg_wout", [P, KC, D])
        merged = sbuf(nc, ctx, "mg_merged", [P, KC, T])
        wg = [sbuf(nc, ctx, f"mg_wg{b}", [P, KC, P]) for b in range(2)]
        wu = [sbuf(nc, ctx, f"mg_wu{b}", [P, NPAIR, P]) for b in range(2)]
        sig = [[sbuf(nc, ctx, f"mg_sig{b}{u}", [P, HALF]) for u in range(2)] for b in range(2)]
        xt = [sbuf(nc, ctx, f"mg_x{u}", [P, D]) for u in range(2)]
        yt = sbuf(nc, ctx, "mg_y", [P, D])
        sq = sbuf(nc, ctx, "mg_sq", [P, D])
        grow = sbuf(nc, ctx, "mg_grow", [P, D])
        ms = [sbuf(nc, ctx, f"mg_ms{u}", [P, 3]) for u in range(2)]
        eps = sbuf(nc, ctx, "mg_eps", [P, 1])
        ps = psum(nc, ctx, "mg_ps", [P, 8, HALF])
        (wout_in, grow_in, wg_in, wu_in, wg1_in, wu1_in, prod_done, sig_done, merged_done, y_done, sq_done,
         root_done, dve_order, x1_ready, eps_set) = (
            kit.sem("mg_" + n) for n in ("wout", "grow", "wg", "wu", "wg1", "wu1", "prod", "sig", "merged", "y", "sq",
                                         "root", "dve", "x1r", "eps"))
        x_in = [kit.sem(f"mg_xin{u}") for u in range(2)]
        stored = [kit.sem(f"mg_st{u}") for u in range(2)]
        block = ctx.enter_context(nc.Block())

        @block.sync
        def _(sp):
            with sp.Fori(0, KC) as d:
                sp.wait_ge(prod_done, 2 * d)
                sp.dma_start(wg[0][:], w_cols(I["w_in"][0], d * P + G_SB, P)).then_inc(wg_in, 16)
                sp.dma_start(wg[1][:], w_cols(I["w_in"][0], d * P + G_SA, P)).then_inc(wg1_in, 16)
                sp.dma_start(wu[0][:], w_cols(I["w_up_sb"][0], d * P, P)).then_inc(wu_in, 16)
                sp.dma_start(wu[1][:], w_cols(I["w_up_sa"][0], d * P, P)).then_inc(wu1_in, 16)
            with sp.Fori(0, NT // 2) as i:
                for u in range(2):
                    sp.wait_ge(stored[u], 16 * i)
                    sp.dma_start(xt[u][:], I["x"][0, bass.ds((i * 2 + u) * P, P), :]).then_inc(x_in[u], 16)

        @block.gpsimd
        def _(pool):
            pool.dma_start(wout[:], I["w_out"][0].rearrange("(k p) f -> p k f", p=P)).then_inc(wout_in, 16)
            pool.dma_start(grow[:], gate_rows[0:8, :].rearrange("(a k) p -> a (k p)", a=1).partition_broadcast(P)).then_inc(grow_in, 16)

        @block.tensor
        def _(pe):
            with pe.Fori(0, KC) as d:
                for s in (wg_in, wg1_in, wu_in, wu1_in):
                    pe.wait_ge(s, 16 * d + 16)
                for half in range(NH):
                    pe.wait_ge(merged_done, 2 * d)
                    bank = 4 * half
                    cols = slice(half * HALF, (half + 1) * HALF)
                    for b in range(2):
                        for k in range(KC):
                            pe.matmul(ps[:, bank + b, :], wg[b][:, k, :], hT[:, k, cols], start=(k == 0), stop=(k == KC - 1))
                    for b, o in enumerate((oT_sb, oT_sa)):
                        for k in range(NPAIR):
                            last = pe.matmul(ps[:, bank + 2 + b, :], wu[b][:, k, :], o[:, k, cols], start=(k == 0), stop=(k == NPAIR - 1))
                    last.then_inc(prod_done, 1)
            pe.wait_ge(merged_done, 2 * KC)
            pe.wait_ge(wout_in, 16)
            for t in range(NT):
                u = t % 2
                if t >= 2:
                    pe.wait_ge(x1_ready, t - 1)
                for half in range(NH):
                    for k in range(KC):
                        last = pe.matmul(ps[:, 4 * u + half, :], merged[:, k, t * P:(t + 1) * P],
                                         wout[:, k, half * HALF:(half + 1) * HALF], start=(k == 0), stop=(k == KC - 1))
                last.then_inc(y_done, 1)

        @block.scalar
        def _(act):
            with act.Fori(0, KC) as d:
                for half in range(NH):
                    act.wait_ge(prod_done, 2 * d + half + 1)
                    act.wait_ge(merged_done, 2 * d)
                    for b in range(2):
                        last = act.activation(sig[b][half][:], ps[:, 4 * half + b, :], ACT.Sigmoid)
                    last.then_inc(sig_done, 1)
            act.wait_ge(eps_set, 1)
            with act.Fori(0, NT // 2) as i:
                for u in range(2):
                    act.wait_ge(y_done, 2 * i + u + 1)
                    act.wait_ge(root_done, 2 * i + u)
                    act.wait_ge(x1_ready, 2 * i)
                    act.activation(sq[:].rearrange("p (h c) -> p h c", h=2), ps[:, 4 * u:4 * u + 2, :], ACT.Square,
                                   accum_out=ms[u][:, 0:1]).then_inc(sq_done, 1)
                    act.wait_ge(sq_done, 2 * i + u + 1)
                    act.activation(ms[u][:, 1:2], ms[u][:, 0:1], ACT.Sqrt, bias=eps[:, 0:1], scale=1.0 / D).then_inc(root_done, 1)
                    act.wait_ge(x1_ready, 2 * i + u + 1)
                    act.dma_start(x1[bass.ds((i * 2 + u) * P, P), :], xt[u][:]).then_inc(stored[u], 16)
            for u in range(2):
                act.wait_ge(stored[u], 16 * (NT // 2))

        @block.vector
        def _(dve):
            dve.memset(eps[:], EPS).then_inc(eps_set, 1)
            with dve.Fori(0, KC) as d:
                link = Linked(dve, dve_order, d * 4)
                for half in range(NH):
                    dve.wait_ge(sig_done, 2 * d + half + 1)
                    cols = slice(half * HALF, (half + 1) * HALF)
                    for b in range(2):
                        link(dve.tensor_tensor(sig[b][half][:], sig[b][half][:], ps[:, 4 * half + 2 + b, :], ALU.mult))
                    dve.tensor_tensor(merged[:, d, cols], sig[0][half][:], sig[1][half][:], ALU.add).then_inc(merged_done, 1)
            dve.wait_ge(grow_in, 16)
            with dve.Fori(0, NT // 2) as i:
                link = Linked(dve, dve_order, KC * 4 + i * 6)
                for u in range(2):
                    dve.wait_ge(root_done, 2 * i + u + 1)
                    link(dve.reciprocal(ms[u][:, 2:3], ms[u][:, 1:2]))
                    dve.wait_ge(x1_ready, 2 * i + u)
                    link(dve.scalar_tensor_tensor(yt[:].rearrange("p (h c) -> p h c", h=2), ps[:, 4 * u:4 * u + 2, :], ms[u][:, 2:3],
                                                  grow[:].rearrange("p (h c) -> p h c", h=2), ALU.mult, ALU.mult))
                    dve.wait_ge(x_in[u], 16 * i + 16)
                    dve.tensor_tensor(xt[u][:], xt[u][:], yt[:], ALU.add).then_inc(x1_ready, 1)
                    link(dve.tensor_copy(ms[u][:, 0:1], eps[:, 0:1]))


def split_stage(nc, kit, hT, hi, lo):
    with ExitStack() as ctx:
        hi_ready, lo_ready = kit.sem("sp_hi"), kit.sem("sp_lo")
        block = ctx.enter_context(nc.Block())

        @block.scalar
        def _(act):
            for k in range(KC):
                act.copy(hi[:, k, :], hT[:, k, :]).then_inc(hi_ready, 1)

        @block.vector
        def _(dve):
            for k in range(KC):
                dve.wait_ge(hi_ready, k + 1)
                dve.tensor_tensor(lo[:, k, :], hT[:, k, :], hi[:, k, :].bitcast(F32), ALU.subtract).then_inc(lo_ready, 1)


def route_stage(nc, kit, I, consts, hT, gT, iT, jT):
    with ExitStack() as ctx:
        wq = sbuf(nc, ctx, "rt_wq", [P, KC, 2 * P])
        keys = sbuf(nc, ctx, "rt_keys", [P, 2, P])
        keysT = sbuf(nc, ctx, "rt_keysT", [P, 2, P])
        qT = sbuf(nc, ctx, "rt_qT", [P, 2, T])
        s = sbuf(nc, ctx, "rt_s", [P, NT * 2, NK])
        work = sbuf(nc, ctx, "rt_work", [P, NT * 2, NK])
        val = sbuf(nc, ctx, "rt_val", [P, NT, 2, PK])
        idx = sbuf(nc, ctx, "rt_idx", [P, NT, 2, PK], U32)
        idxf = sbuf(nc, ctx, "rt_idxf", [P, NT, 2, PK])
        cand = sbuf(nc, ctx, "rt_cand", [P, NT, PK, PK])
        cwork = sbuf(nc, ctx, "rt_cwork", [P, NT, PK * PK])
        topv = sbuf(nc, ctx, "rt_topv", [P, NT, PK])
        topp = sbuf(nc, ctx, "rt_topp", [P, NT, PK], U32)
        part = sbuf(nc, ctx, "rt_part", [P, 2, NT, PK], U32)
        partf = sbuf(nc, ctx, "rt_partf", [P, 2, NT, PK])
        hot = sbuf(nc, ctx, "rt_hot", [P, NT, PK, PK])
        es = sbuf(nc, ctx, "rt_es", [P, NT, PK])
        ex = sbuf(nc, ctx, "rt_ex", [P, NT, PK])
        tot = sbuf(nc, ctx, "rt_tot", [P, NT, 2])
        out = [sbuf(nc, ctx, f"rt_out{n}", [P, NT, PH * PK]) for n in range(3)]
        ps_q = psum(nc, ctx, "rt_pq", [P, 2, HALF])
        ps_k = psum(nc, ctx, "rt_pk", [P, HALF])
        ps_s = psum(nc, ctx, "rt_ps", [P, NT * 2, NK])
        (wq_in, keys_in, k_done, k_read, q_done, q_read, s_done, s_read, s_used, exp_in, exp_done, dve_order,
         chosen, turned, kept) = (
            kit.sem("rt_" + n) for n in ("wq", "keys", "kd", "kr", "qd", "qr", "sd", "sr", "su", "ei", "ed", "dve",
                                         "chosen", "turned", "kept"))
        block = ctx.enter_context(nc.Block())

        @block.sync
        def _(sp):
            with sp.Fori(0, PH) as h:
                sp.wait_ge(q_done, 2 * h)
                sp.dma_start(wq[:], w_cols(I["w_peer_query"][0], h * (2 * P), 2 * P)).then_inc(wq_in, 16)
                sp.dma_start(keys[:], I["peer_sub_keys"][0, bass.ds(h, 1)].rearrange("a b k d -> k (a b) d")).then_inc(keys_in, 16)

        @block.tensor
        def _(pe):
            with pe.Fori(0, PH) as h:
                pe.wait_ge(keys_in, 16 * h + 16)
                for b in range(2):
                    last = pe.transpose(ps_k[:, b * P:(b + 1) * P], keys[:, b, :], consts["ident"][:, :])
                last.then_inc(k_done, 1)
                pe.wait_ge(wq_in, 16 * h + 16)
                for b in range(2):
                    pe.wait_ge(q_read, 2 * h + b)
                    project_T(pe, ps_q, wq[:, :, b * P:(b + 1) * P], hT).then_inc(q_done, 1)
                pe.wait_ge(k_read, h + 1)
                pe.wait_ge(q_read, 2 * h + 2)
                pe.wait_ge(s_read, h)
                for t in range(NT):
                    for b in range(2):
                        last = pe.matmul(ps_s[:, 2 * t + b, :], qT[:, b, t * P:(t + 1) * P], keysT[:, b, :], start=True, stop=True)
                last.then_inc(s_done, 1)
            pe.wait_ge(chosen, PH)
            for t in range(NT):
                pe.wait_ge(kept, t)
                for n in range(3):
                    last = pe.transpose(ps_k[:, n * P:(n + 1) * P], out[n][:, t, :], consts["ident"][:, :])
                last.then_inc(turned, 1)

        @block.scalar
        def _(act):
            with act.Fori(0, PH) as h:
                act.wait_ge(k_done, h + 1)
                act.wait_ge(s_done, h)
                act.copy(keysT[:].rearrange("p b k -> p (b k)"), ps_k[:, 0:2 * P]).then_inc(k_read, 1)
                for b in range(2):
                    act.wait_ge(q_done, 2 * h + b + 1)
                    act.copy(qT[:, b, :], flat(ps_q)).then_inc(q_read, 1)
                act.wait_ge(s_done, h + 1)
                act.wait_ge(s_used, h)
                act.copy(s[:].rearrange("p r k -> p (r k)"), ps_s[:].rearrange("p r k -> p (r k)")).then_inc(s_read, 1)
                act.wait_ge(exp_in, h + 1)
                act.activation(ex[:], es[:], ACT.Exp).then_inc(exp_done, 1)
            for t in range(NT):
                act.wait_ge(turned, t + 1)
                for n, dst in enumerate((gT, iT, jT)):
                    last = act.copy(dst[:, t * P:(t + 1) * P], ps_k[:, n * P:(n + 1) * P])
                last.then_inc(kept, 1)

        @block.vector
        def _(dve):
            LINKS = 22
            with dve.Fori(0, PH) as h:
                link = Linked(dve, dve_order, h * LINKS, apart=True)

                def best16(rows, src, other, v, ix):
                    for step in range(5):
                        for r in range(rows):
                            if step == 0:
                                ins = dve.max(v(r)[:, 0:8], src(r))
                            elif step == 1:
                                ins = dve.max_index(ix(r)[:, 0:8], v(r)[:, 0:8], src(r))
                            elif step == 2:
                                ins = dve.match_replace(other(r), v(r)[:, 0:8], src(r), TAKEN)
                            elif step == 3:
                                ins = dve.max(v(r)[:, 8:16], other(r))
                            else:
                                ins = dve.max_index(ix(r)[:, 8:16], v(r)[:, 8:16], other(r))
                        if not (step == 4 and rows > NT):
                            link(ins)
                        else:
                            ins.then_inc(s_used, 1)

                dve.wait_ge(s_read, h + 1)
                dve.nop(nofuse=True)
                best16(2 * NT, lambda r: s[:, r, :], lambda r: work[:, r, :], lambda r: val[:, r // 2, r % 2, :],
                       lambda r: idx[:, r // 2, r % 2, :])
                dve.wait_ge(s_used, h + 1)
                link(dve.tensor_copy(idxf[:], idx[:]))
                link(dve.tensor_tensor(cand[:], val[:, :, 0, :].unsqueeze(3).broadcast_to([P, NT, PK, PK]),
                                       val[:, :, 1, :].unsqueeze(2).broadcast_to([P, NT, PK, PK]), ALU.add))
                best16(NT, lambda r: cand[:, r, :, :].rearrange("p a b -> p (a b)"), lambda r: cwork[:, r, :],
                       lambda r: topv[:, r, :], lambda r: topp[:, r, :])
                dve.wait_ge(exp_done, h)
                dve.tensor_tensor(es[:], topv[:], topv[:, :, 0:1].broadcast_to([P, NT, PK]), ALU.subtract).then_inc(exp_in, 1)
                link(dve.tensor_scalar(part[:, 0], topp[:], 4, None, ALU.logical_shift_right))
                link(dve.tensor_scalar(part[:, 1], topp[:], 15, None, ALU.bitwise_and))
                link(dve.tensor_copy(partf[:], part[:]))
                for b in range(2):
                    link(dve.tensor_tensor(hot[:], partf[:, b].unsqueeze(3).broadcast_to([P, NT, PK, PK]),
                                           consts["iota16"].unsqueeze(1).unsqueeze(1).broadcast_to([P, NT, PK, PK]), ALU.is_equal))
                    link(dve.tensor_tensor(hot[:], hot[:], idxf[:, :, b, :].unsqueeze(2).broadcast_to([P, NT, PK, PK]), ALU.mult))
                    link(dve.tensor_reduce(out[1 + b][:, :, bass.ds(h * PK, PK)], hot[:], AX.X, ALU.add))
                dve.wait_ge(exp_done, h + 1)
                link(dve.tensor_reduce(tot[:, :, 0:1], ex[:], AX.X, ALU.add))
                link(dve.reciprocal(tot[:, :, 1:2], tot[:, :, 0:1]))
                dve.tensor_tensor(out[0][:, :, bass.ds(h * PK, PK)], ex[:], tot[:, :, 1:2].broadcast_to([P, NT, PK]),
                                  ALU.mult).then_inc(chosen, 1)
                dve.wait_ge(chosen, h + 1)
                if link.n != LINKS:
                    raise ValueError(link.n)


SPREAD_T = 64


def spread_stage(nc, kit, consts, gT, iT, jT, G):
    GROUP = 4
    PAIRS = SPREAD_T // GROUP // 2
    with ExitStack() as ctx:
        first = [sbuf(nc, ctx, f"gs_first{u}", [P, GROUP, NK]) for u in range(2)]
        second = [sbuf(nc, ctx, f"gs_second{u}", [P, GROUP, NK]) for u in range(2)]
        piece = [sbuf(nc, ctx, f"gs_piece{u}", [P, NK, SPREAD_T]) for u in range(2)]
        ps = [psum(nc, ctx, f"gs_ps{u}", [P, GROUP, NK]) for u in range(2)]
        hot_done, prod_done, copied = kit.sem("gs_hot"), kit.sem("gs_prod"), kit.sem("gs_copied")
        stored = [kit.sem(f"gs_st{u}") for u in range(2)]
        NP = T // SPREAD_T // 2
        block = ctx.enter_context(nc.Block())

        @block.vector
        def _(dve):
            with dve.Fori(0, T // (2 * GROUP)) as q:
                for u in range(2):
                    dve.wait_ge(prod_done, 2 * q)
                    for n in range(GROUP):
                        tok = q * (2 * GROUP) + (u * GROUP + n)
                        dve.tensor_scalar(first[u][:, n, :], consts["iota"][:, :], iT[:, bass.ds(tok, 1)],
                                          gT[:, bass.ds(tok, 1)], ALU.is_equal, ALU.mult)
                        last = dve.tensor_scalar(second[u][:, n, :], consts["iota"][:, :], jT[:, bass.ds(tok, 1)], None,
                                                 ALU.is_equal)
                    last.then_inc(hot_done, 1)

        @block.tensor
        def _(pe):
            with pe.Fori(0, T // (2 * GROUP)) as q:
                for u in range(2):
                    pe.wait_ge(hot_done, 2 * q + u + 1)
                    pe.wait_ge(copied, 2 * q)
                    for n in range(GROUP):
                        last = pe.matmul(ps[u][:, n, :], first[u][:, n, :], second[u][:, n, :], start=True, stop=True)
                    last.then_inc(prod_done, 1)

        @block.scalar
        def _(act):
            with act.Fori(0, NP) as c:
                for b in range(2):
                    act.wait_ge(stored[b], 16 * c)
                    with act.Fori(0, PAIRS) as q:
                        for u in range(2):
                            act.wait_ge(prod_done, ((c * 2 + b) * PAIRS + q) * 2 + (u + 1))
                            act.copy(piece[b][:, :, bass.ds((q * 2 + u) * GROUP, GROUP)].rearrange("p j t -> p t j"),
                                     ps[u][:]).then_inc(copied, 1)

        @block.sync
        def _(sp):
            with sp.Fori(0, NP) as c:
                for b in range(2):
                    sp.wait_ge(copied, (c * 2 + (b + 1)) * (2 * PAIRS))
                    sp.dma_start(G[bass.ds(c * 2 + b, 1)].rearrange("a i j t -> (a i) j t"), piece[b][:]).then_inc(stored[b], 16)
            for b in range(2):
                sp.wait_ge(stored[b], 16 * NP)


def experts_stage(nc, kit, I, consts, hi, lo, G, acc):
    JG = 2
    NG = NK // JG
    CH = T // SPREAD_T
    win_d = I["peer_expert_in"][0].rearrange("(i j) d -> i j d", j=NK)
    wout_d = I["peer_expert_out"][0].rearrange("(i j) d -> i j d", j=NK)
    TURNED, A_DONE, GELU, WEIGHTED, ALO, Y, ADDED = 1, 2, 1, 4, 1, 16, 3
    with ExitStack() as ctx:
        win = [sbuf(nc, ctx, f"ex_win{u}", [P, D]) for u in range(2)]
        win_hi = [sbuf(nc, ctx, f"ex_whi{u}", [P, KC, P], F32R) for u in range(2)]
        win_lo = [sbuf(nc, ctx, f"ex_wlo{u}", [P, KC, P], F32R) for u in range(2)]
        wout = [sbuf(nc, ctx, f"ex_wout{u}", [P, D]) for u in range(JG)]
        wout_hi = sbuf(nc, ctx, "ex_ohi", [P, JG, D], F32R)
        wout_lo = sbuf(nc, ctx, "ex_olo", [P, JG, D], F32R)
        g = [sbuf(nc, ctx, f"ex_g{u}", [P, CH, JG, SPREAD_T]) for u in range(2)]
        a = [sbuf(nc, ctx, f"ex_a{u}", [P, HALF]) for u in range(2)]
        a_hi = [sbuf(nc, ctx, f"ex_ahi{u}", [P, JG, T], F32R) for u in range(2)]
        a_lo = [sbuf(nc, ctx, f"ex_alo{u}", [P, JG, T], F32R) for u in range(2)]
        ps_w = psum(nc, ctx, "ex_pw", [P, KC, P])
        ps_a = [psum(nc, ctx, f"ex_pa{u}", [P, HALF]) for u in range(2)]
        ps_y = [psum(nc, ctx, f"ex_py{u}", [P, HALF]) for u in range(4)]
        win_in = [kit.sem(f"ex_win_in{u}") for u in range(2)]
        g_in = [kit.sem(f"ex_g_in{u}") for u in range(2)]
        wout_in = [kit.sem(f"ex_wout_in{u}") for u in range(JG)]
        (turned, whi_done, wlo_done, a_done, gelu_done, weighted, ahi_done, alo_done, ohi_done, olo_done, y_done,
         y_added) = (kit.sem("ex_" + n) for n in ("wt", "whi", "wlo", "a", "gelu", "wtd", "ahi", "alo", "ohi", "olo",
                                                  "y", "ya"))
        block = ctx.enter_context(nc.Block())

        def all_groups(eng, group):
            group(0, 0, True, False)
            group(1, 1, False, False)
            with eng.Fori(1, NG // 2 - 1) as gg:
                group(gg * 2, 0, False, False)
                group(gg * 2 + 1, 1, False, False)
            group(NG - 2, 0, False, False)
            group(NG - 1, 1, False, True)

        @block.sync
        def _(sp):
            def load(grp, u, first, last):
                for j in range(JG):
                    sp.wait_ge(turned, grp * 2 + j)
                    sp.dma_start(win[j][:], win_d[:, bass.ds(grp * JG + j, 1), :].rearrange("i a d -> i (a d)")).then_inc(win_in[j], 16)
                sp.wait_ge(weighted, grp * 4)
                sp.dma_start(g[u][:].rearrange("i c j t -> i c (j t)"),
                             G[:, :, bass.ds(grp * JG, JG), :].rearrange("c i j t -> i c (j t)")).then_inc(g_in[u], 16)
                for j in range(JG):
                    sp.wait_ge(olo_done, grp * 2)
                    sp.dma_start(wout[j][:], wout_d[:, bass.ds(grp * JG + j, 1), :].rearrange("i a d -> i (a d)")).then_inc(wout_in[j], 16)

            all_groups(sp, load)

        @block.tensor
        def _(pe):
            def turn_win(grp, j):
                pe.wait_ge(win_in[j], grp * 16 + 16)
                pe.wait_ge(wlo_done, grp * 2 + j)
                for k in range(KC):
                    last = pe.transpose(ps_w[:, k, :], win[j][:, k * P:(k + 1) * P], consts["ident"][:, :])
                last.then_inc(turned, 1)

            def activations(grp, j):
                pe.wait_ge(wlo_done, grp * 2 + (j + 1))
                for half in range(NH):
                    pe.wait_ge(gelu_done, grp * 4 + (2 * j + half))
                    cols = slice(half * HALF, (half + 1) * HALF)
                    for k in range(KC):
                        pe.matmul(ps_a[half][:, :], win_hi[j][:, k, :], hi[:, k, cols], start=(k == 0), stop=False)
                        pe.matmul(ps_a[half][:, :], win_hi[j][:, k, :], lo[:, k, cols], start=False, stop=False)
                        last = pe.matmul(ps_a[half][:, :], win_lo[j][:, k, :], hi[:, k, cols], start=False, stop=(k == KC - 1))
                    last.then_inc(a_done, 1)

            def outputs(grp, u):
                pe.wait_ge(alo_done, grp * 4 + (4 + ALO))
                pe.wait_ge(olo_done, grp * 2 + 2)
                for n in range(2 * NT):
                    t, half = n // 2, n % 2
                    pe.wait_ge(y_added, grp * 16 + n)
                    cols = slice(half * HALF, (half + 1) * HALF)
                    rows = slice(t * P, (t + 1) * P)
                    y = ps_y[n % 4][:, :]
                    for j in range(JG):
                        pe.matmul(y, a_hi[u][:, j, rows], wout_hi[:, j, cols], start=(j == 0), stop=False)
                        pe.matmul(y, a_hi[u][:, j, rows], wout_lo[:, j, cols], start=False, stop=False)
                        last = pe.matmul(y, a_lo[u][:, j, rows], wout_hi[:, j, cols], start=False, stop=(j == JG - 1))
                    last.then_inc(y_done, 1)

            def group(grp, u, first, last):
                turn_win(grp, 1)
                activations(grp, 0)
                if not last:
                    turn_win(grp + 1, 0)
                activations(grp, 1)
                if not first:
                    outputs(grp - 1, 1 - u)

            pe.sem_inc(turned, TURNED)
            pe.sem_inc(a_done, A_DONE)
            pe.sem_inc(y_done, Y)
            turn_win(0, 0)
            all_groups(pe, group)
            outputs(NG - 1, 1)

        @block.scalar
        def _(act):
            def split_win(grp, j):
                act.wait_ge(turned, grp * 2 + (j + 1 + TURNED))
                act.wait_ge(a_done, grp * 4 + 2 * j)
                act.copy(win_hi[j][:], ps_w[:]).then_inc(whi_done, 1)

            def split_wout(grp):
                act.wait_ge(y_done, grp * 16 + Y)
                for j in range(JG):
                    act.wait_ge(wout_in[j], grp * 16 + 16)
                    act.copy(wout_hi[:, j, :], wout[j][:]).then_inc(ohi_done, 1)

            def gelu_part(grp, u, j):
                for half in range(NH):
                    e = 2 * j + half
                    act.wait_ge(a_done, grp * 4 + (e + 1 + A_DONE))
                    act.wait_ge(alo_done, grp * 4 + e)
                    act.activation(a[half][:], ps_a[half][:, :], ACT.Gelu).then_inc(gelu_done, 1)
                act.wait_ge(y_done, grp * 16)
                for half in range(NH):
                    e = 2 * j + half
                    act.wait_ge(weighted, grp * 4 + (e + 1 + WEIGHTED))
                    act.copy(a_hi[u][:, j, half * HALF:(half + 1) * HALF], a[half][:]).then_inc(ahi_done, 1)

            def group(grp, u, first, last):
                split_win(grp, 1)
                if not first:
                    split_wout(grp - 1)
                gelu_part(grp, u, 0)
                if not last:
                    split_win(grp + 1, 0)
                gelu_part(grp, u, 1)

            act.sem_inc(gelu_done, GELU)
            split_win(0, 0)
            all_groups(act, group)
            split_wout(NG - 1)

        @block.vector
        def _(dve):
            def split_win(grp, j):
                dve.wait_ge(whi_done, grp * 2 + (j + 1))
                dve.tensor_tensor(win_lo[j][:], ps_w[:], win_hi[j][:].bitcast(F32), ALU.subtract).then_inc(wlo_done, 1)

            def split_wout(grp):
                for j in range(JG):
                    dve.wait_ge(ohi_done, grp * 2 + (j + 1))
                    dve.tensor_tensor(wout_lo[:, j, :], wout[j][:], wout_hi[:, j, :].bitcast(F32), ALU.subtract).then_inc(olo_done, 1)

            def weigh(grp, gg_in, u, j):
                dve.wait_ge(g_in[u], gg_in)
                for half in range(NH):
                    dve.wait_ge(gelu_done, grp * 4 + (2 * j + half + 1 + GELU))
                    v = a[half][:].rearrange("p (c t) -> p c t", t=SPREAD_T)
                    dve.tensor_tensor(v, v, g[u][:, half * CH // 2:(half + 1) * CH // 2, j, :], ALU.mult).then_inc(weighted, 1)
                for half in range(NH):
                    dve.wait_ge(ahi_done, grp * 4 + (2 * j + half + 1))
                    part = slice(half * HALF, (half + 1) * HALF)
                    dve.tensor_tensor(a_lo[u][:, j, part], a[half][:], a_hi[u][:, j, part].bitcast(F32), ALU.subtract).then_inc(alo_done, 1)

            def add_outputs(grp, first):
                if not first:
                    dve.wait_ge(y_added, grp * 16 + ADDED)
                for n in range(2 * NT):
                    dve.wait_ge(y_done, grp * 16 + (n + 1 + Y))
                    dst = acc[:, n // 2, (n % 2) * HALF:(n % 2 + 1) * HALF]
                    if first:
                        ins = dve.tensor_copy(dst, ps_y[n % 4][:, :])
                    else:
                        ins = dve.tensor_tensor(dst, dst, ps_y[n % 4][:, :], ALU.add)
                    ins.then_inc(y_added, 1)

            def group(grp, u, first, last):
                split_win(grp, 1)
                if not first:
                    split_wout(grp - 1)
                g_value = (grp - u) * 8 + 16
                weigh(grp, g_value, u, 0)
                if not last:
                    split_win(grp + 1, 0)
                weigh(grp, g_value, u, 1)
                if not first:
                    add_outputs(grp - 1, isinstance(grp, int) and grp == 1)

            dve.sem_inc(weighted, WEIGHTED)
            dve.sem_inc(alo_done, ALO)
            dve.sem_inc(y_added, ADDED)
            split_win(0, 0)
            all_groups(dve, group)
            split_wout(NG - 1)
            add_outputs(NG - 1, False)


def final_stage(nc, kit, acc, gate_rows, x1, out):
    with ExitStack() as ctx:
        grow = sbuf(nc, ctx, "fn_grow", [P, D])
        xt = [sbuf(nc, ctx, f"fn_x{u}", [P, D]) for u in range(NT)]
        sq = sbuf(nc, ctx, "fn_sq", [P, D])
        ms = [sbuf(nc, ctx, f"fn_ms{u}", [P, 3]) for u in range(NT)]
        eps = sbuf(nc, ctx, "fn_eps", [P, 1])
        grow_in, x_in, eps_set, sq_done, root_done, dve_order, ready, stored = (
            kit.sem("fn_" + n) for n in ("grow", "x", "eps", "sq", "root", "dve", "ready", "stored"))
        block = ctx.enter_context(nc.Block())

        @block.sync
        def _(sp):
            sp.dma_start(grow[:], gate_rows[8:16, :].rearrange("(a k) p -> a (k p)", a=1).partition_broadcast(P)).then_inc(grow_in, 16)
            for t in range(NT):
                sp.dma_start(xt[t][:], x1[t * P:(t + 1) * P, :]).then_inc(x_in, 16)
            for t in range(NT):
                sp.wait_ge(ready, t + 1)
                sp.dma_start(out[0, t * P:(t + 1) * P, :], xt[t][:]).then_inc(stored, 16)
            sp.wait_ge(stored, 16 * NT)

        @block.scalar
        def _(act):
            act.wait_ge(eps_set, 1)
            for t in range(NT):
                if t:
                    act.wait_ge(sq_done, t)
                act.activation(sq[:], acc[:, t, :], ACT.Square, accum_out=ms[t][:, 0:1]).then_inc(sq_done, 1)
            act.wait_ge(sq_done, NT)
            for t in range(NT):
                act.activation(ms[t][:, 1:2], ms[t][:, 0:1], ACT.Sqrt, bias=eps[:, 0:1], scale=1.0 / D).then_inc(root_done, 1)

        @block.vector
        def _(dve):
            dve.memset(eps[:], EPS).then_inc(eps_set, 1)
            link = Linked(dve, dve_order)
            dve.wait_ge(grow_in, 16)
            dve.wait_ge(x_in, 16 * NT)
            for t in range(NT):
                dve.wait_ge(root_done, t + 1)
                link(dve.reciprocal(ms[t][:, 2:3], ms[t][:, 1:2]))
                link(dve.scalar_tensor_tensor(acc[:, t, :], acc[:, t, :], ms[t][:, 2:3], grow[:], ALU.mult, ALU.mult))
                dve.tensor_tensor(xt[t][:], xt[t][:], acc[:, t, :], ALU.add).then_inc(ready, 1)


def hybrid_block(nc, I, out, probe=None):
    kit = Kit(nc)
    hbm = lambda name, shape: nc.dram_tensor(name, shape, F32, kind="Internal").ap()
    gate_rows = hbm("gate_rows_scratch", [16, P])
    x1 = hbm("x1_scratch", [T, D])
    G = hbm("g_scratch", [T // SPREAD_T, P, NK, SPREAD_T])
    total = sum(CONST_COLS.values())
    with kit.stack, ExitStack() as whole:
        all_consts = sbuf(nc, whole, "consts_sb", [P, total])
        consts, c0 = {"all": all_consts}, 0
        for name, n in CONST_COLS.items():
            consts[name] = all_consts[:, c0:c0 + n]
            c0 += n
        cols = sbuf(nc, whole, "ada_cols", [P, 32])
        ada_stage(nc, kit, I, consts, cols, gate_rows)
        with ExitStack() as mix:
            hT = sbuf(nc, mix, "hT", [P, KC, T])
            oT_sb = sbuf(nc, mix, "oT_sb", [P, NPAIR, T])
            oT_sa = sbuf(nc, mix, "oT_sa", [P, NPAIR, T])
            pre_norm_stage(nc, kit, "n1", I["x"][0], consts, cols[:, 0:8], cols[:, 8:16], hT)
            if probe == "hT":
                return dump(nc, kit, hT, out)
            with ExitStack() as att:
                cosT = sbuf(nc, att, "cosT", [P, T])
                sinT = sbuf(nc, att, "sinT", [P, T])
                scores = sbuf(nc, att, "scores", [P, NT, T])
                indexer_stage(nc, kit, I, consts, hT, cosT, sinT, scores)
                if probe == "scores":
                    return dump(nc, kit, scores, out)
                stick_stage(nc, kit, I, consts, hT, oT_sb)
                if probe == "oT_sb":
                    return dump(nc, kit, oT_sb, out)
                select_stage(nc, kit, consts, scores)
                sparse_stage(nc, kit, I, consts, hT, cosT, sinT, scores, oT_sa)
                if probe == "oT_sa":
                    return dump(nc, kit, oT_sa, out)
            merge_stage(nc, kit, I, hT, oT_sb, oT_sa, gate_rows, x1)
        with ExitStack() as peer:
            acc = sbuf(nc, peer, "acc", [P, NT, D])
            hi = sbuf(nc, peer, "h_hi", [P, KC, T], F32R)
            lo = sbuf(nc, peer, "h_lo", [P, KC, T], F32R)
            with ExitStack() as rs:
                gT = sbuf(nc, rs, "gT", [P, T])
                iT = sbuf(nc, rs, "iT", [P, T])
                jT = sbuf(nc, rs, "jT", [P, T])
                pre_norm_stage(nc, kit, "n2", x1, consts, cols[:, 16:24], cols[:, 24:32], acc)
                split_stage(nc, kit, acc, hi, lo)
                with ExitStack() as only_route:
                    route_stage(nc, kit, I, consts, acc, gT, iT, jT)
                if probe == "gT":
                    return dump(nc, kit, [gT, iT, jT], out)
                spread_stage(nc, kit, consts, gT, iT, jT, G)
            experts_stage(nc, kit, I, consts, hi, lo, G, acc)
            final_stage(nc, kit, acc, gate_rows, x1, out)


_INS = ["x", "c", "positions", "w_ada", "b_ada", "g_pre_mix", "g_post_mix", "w_in", "w_up_sb", "w_up_sa", "w_out",
        "g_pre_ffn", "g_post_ffn", "w_peer_query", "peer_sub_keys", "peer_expert_in", "peer_expert_out"]


def kernel(**inputs):
    import concourse.bacc as _bacc
    from concourse.bass_utils import run_bass_kernel_spmd as _run

    nc = _bacc.Bacc("TRN2", target_bir_lowering=False, num_devices=1)
    arrays, args = {}, {}
    given = {name: np.ascontiguousarray(inputs[name]) for name in _INS}
    given["consts"] = shape_constants()
    for name, a in given.items():
        arrays[f"in_{name}_dram"] = a
        args[name] = nc.dram_tensor(f"in_{name}_dram", a.shape, mybir.dt.from_np(a.dtype), kind="ExternalInput").ap()
    out = nc.dram_tensor("out_dram", (1, T, D), F32, kind="ExternalOutput").ap()
    hybrid_block(nc, args, out)
    r = _run(nc, [arrays], core_ids=[0])
    return r.results[0]["out_dram"]
```
